# Optimizing a Trainium2 kernel written in Bass

```python
import jax, jax.numpy as jnp
from jax import lax
import numpy as np

D_MODEL = 1024
BATCH = 1
SEQ = 512
DEPTH = 2

SB_HEAD_DIM = 64
SB_HEADS = D_MODEL // 128
SB_WIDTH = SB_HEADS * SB_HEAD_DIM
BLOCK_Q = 128
RET_HEADS = D_MODEL // 256
RET_QK_DIM = 128
RET_V_DIM = 2 * RET_QK_DIM
RET_QK_WIDTH = RET_HEADS * RET_QK_DIM
RET_V_WIDTH = RET_HEADS * RET_V_DIM
RET_CHUNK = 128
ROPE_BASE = 10000.0
SPLIT_SIZES = (SB_WIDTH, SB_WIDTH, SB_WIDTH,
               RET_QK_WIDTH, RET_QK_WIDTH, RET_V_WIDTH,
               RET_V_WIDTH,
               2 * D_MODEL)
IN_COLS = sum(SPLIT_SIZES)
SPLIT_POINTS = tuple(int(v) for v in np.cumsum(SPLIT_SIZES)[:-1])
D_FF = ((8 * D_MODEL // 3 + 127) // 128) * 128
CONV_WIDTH = 3
EPS = 1e-6

kernel_name = "hybrid_stickbreaking_retention_convffn"

def rms_norm(x, g):
    xf = x.astype(jnp.float32)
    y = xf * lax.rsqrt(jnp.mean(xf * xf, axis=-1, keepdims=True) + EPS)
    return (y * g.astype(jnp.float32)).astype(x.dtype)

def rotary(t, pos):
    half = t.shape[-1] // 2
    inv = ROPE_BASE ** (-jnp.arange(half, dtype=jnp.float32) / half)
    ang = pos[:, None] * inv[None, :]
    cos = jnp.cos(ang)[None, :, None, :]
    sin = jnp.sin(ang)[None, :, None, :]
    t = t.astype(jnp.float32)
    t1, t2 = t[..., :half], t[..., half:]
    return jnp.concatenate([t1 * cos - t2 * sin, t1 * sin + t2 * cos], axis=-1)

def stick_breaking_attention(q, k, v):
    S = q.shape[2]
    scale = q.shape[-1] ** -0.5
    outs = []
    for i in range(S // BLOCK_Q):
        end = (i + 1) * BLOCK_Q
        qs = q[:, :, i * BLOCK_Q:end]
        kk, vv = k[:, :, :end], v[:, :, :end]
        z = jnp.einsum('bhqd,bhkd->bhqk', qs, kk).astype(jnp.float32) * scale
        t_idx = i * BLOCK_Q + jnp.arange(BLOCK_Q)[:, None]
        s_idx = jnp.arange(end)[None, :]
        mask = s_idx < t_idx
        log_keep = jnp.where(mask, jax.nn.log_sigmoid(-z), 0.0)
        suffix = lax.cumsum(log_keep, axis=3, reverse=True) - log_keep
        a = jnp.where(mask, jnp.exp(jax.nn.log_sigmoid(z) + suffix), 0.0)
        outs.append(jnp.einsum('bhqk,bhkd->bhqd', a, vv.astype(jnp.float32)))
    return jnp.concatenate(outs, axis=2)

def retention_chunkwise(q, k, v, log_gamma):
    B, H, S, dk = q.shape
    dv = v.shape[-1]
    C = RET_CHUNK
    nC = S // C
    qc = q.reshape(B, H, nC, C, dk)
    kc = k.reshape(B, H, nC, C, dk)
    vc = v.reshape(B, H, nC, C, dv)
    pos = jnp.arange(C, dtype=jnp.float32)
    lg = log_gamma[:, None, None]
    diff = pos[:, None] - pos[None, :]
    decay = jnp.where(diff >= 0, jnp.exp(jnp.maximum(diff, 0.0) * lg), 0.0)
    scores = jnp.einsum('bhcnd,bhcmd->bhcnm', qc, kc) * decay[None, :, None]
    inner = jnp.einsum('bhcnm,bhcme->bhcne', scores, vc)
    zeta = jnp.exp((C - 1 - pos)[None, :] * log_gamma[:, None])
    xi = jnp.exp((pos + 1)[None, :] * log_gamma[:, None])
    chunk_decay = jnp.exp(C * log_gamma)[None, :, None, None]
    kv = jnp.einsum('bhcmd,bhcme->cbhde', kc * zeta[None, :, None, :, None], vc)

    def step(state, kv_c):
        return state * chunk_decay + kv_c, state

    _, prev_states = lax.scan(step, jnp.zeros((B, H, dk, dv), jnp.float32), kv)
    cross = jnp.einsum('bhcnd,cbhde->bhcne', qc, prev_states) * xi[None, :, None, :, None]
    return (inner + cross).reshape(B, H, S, dv)

def head_group_norm(o, g):
    mu = jnp.mean(o, axis=-1, keepdims=True)
    var = jnp.mean(jnp.square(o - mu), axis=-1, keepdims=True)
    y = (o - mu) * lax.rsqrt(var + EPS)
    B, S = o.shape[:2]
    return y.reshape(B, S, -1) * g.astype(jnp.float32)

def hybrid_mixer(x, norm_g, w_in, b_gate, sb_w_out, ret_norm_g, ret_w_out, w_o):
    B, S, _ = x.shape
    h = rms_norm(x, norm_g)
    proj = h @ w_in
    q_sb, k_sb, v_sb, q_r, k_r, v_r, g_r, gates = jnp.split(proj, SPLIT_POINTS, axis=-1)

    def heads(t, n):
        return t.reshape(B, S, n, -1).transpose(0, 2, 1, 3)

    o_sb = stick_breaking_attention(heads(q_sb, SB_HEADS), heads(k_sb, SB_HEADS), heads(v_sb, SB_HEADS))
    o_sb = o_sb.transpose(0, 2, 1, 3).reshape(B, S, SB_WIDTH).astype(x.dtype)
    y_a = o_sb @ sb_w_out

    pos = jnp.arange(S, dtype=jnp.float32)
    qr = rotary(q_r.reshape(B, S, RET_HEADS, RET_QK_DIM), pos).transpose(0, 2, 1, 3)
    kr = (rotary(k_r.reshape(B, S, RET_HEADS, RET_QK_DIM), pos) * RET_QK_DIM ** -0.5).transpose(0, 2, 1, 3)
    vr = heads(v_r, RET_HEADS).astype(jnp.float32)
    log_gamma = jnp.log1p(-jnp.exp2(-5.0 - jnp.arange(RET_HEADS, dtype=jnp.float32)))
    o_r = retention_chunkwise(qr, kr, vr, log_gamma).transpose(0, 2, 1, 3)
    o_r = head_group_norm(o_r, ret_norm_g) * jax.nn.silu(g_r.astype(jnp.float32))
    y_b = o_r.astype(x.dtype) @ ret_w_out

    gate = jax.nn.sigmoid((gates + b_gate).astype(jnp.float32))
    g_a, g_b = gate[..., :D_MODEL], gate[..., D_MODEL:]
    merged = (g_a * y_a.astype(jnp.float32) + g_b * y_b.astype(jnp.float32)).astype(x.dtype)
    return merged @ w_o

def conv_ffn(x, norm_g, w_up, conv_w, conv_b, w_down):
    h = rms_norm(x, norm_g)
    a, b = jnp.split(h @ w_up, 2, axis=-1)
    a = lax.conv_general_dilated(a, conv_w[:, None, :], window_strides=(1,),
                                 padding=[(CONV_WIDTH - 1, 0)],
                                 dimension_numbers=('NWC', 'WIO', 'NWC'),
                                 feature_group_count=D_FF) + conv_b
    return (jax.nn.silu(a) * b) @ w_down

def setup_inputs(seed: int = 0) -> dict:
    key = jax.random.key(seed)
    ks = jax.random.split(key, 16)
    f32 = jnp.float32

    def dense(k, shape, fan_in):
        return jax.random.normal(k, shape, f32) * fan_in ** -0.5

    def gain(k, shape):
        return 1.0 + 0.02 * jax.random.normal(k, shape, f32)

    return {
        "x": jax.random.normal(ks[0], (BATCH, SEQ, D_MODEL), f32),
        "attn_norm": gain(ks[1], (DEPTH, D_MODEL)),
        "w_in": dense(ks[2], (DEPTH, D_MODEL, IN_COLS), D_MODEL),
        "b_gate": 0.02 * jax.random.normal(ks[3], (DEPTH, 2 * D_MODEL), f32),
        "sb_w_out": dense(ks[4], (DEPTH, SB_WIDTH, D_MODEL), SB_WIDTH),
        "ret_norm": gain(ks[5], (DEPTH, RET_V_WIDTH)),
        "ret_w_out": dense(ks[6], (DEPTH, RET_V_WIDTH, D_MODEL), RET_V_WIDTH),
        "w_o": dense(ks[7], (DEPTH, D_MODEL, D_MODEL), D_MODEL),
        "ffn_norm": gain(ks[8], (DEPTH, D_MODEL)),
        "w_up": dense(ks[9], (DEPTH, D_MODEL, 2 * D_FF), D_MODEL),
        "conv_w": dense(ks[10], (DEPTH, CONV_WIDTH, D_FF), CONV_WIDTH),
        "conv_b": 0.02 * jax.random.normal(ks[11], (DEPTH, D_FF), f32),
        "w_down": dense(ks[12], (DEPTH, D_FF, D_MODEL), D_FF),
        "final_norm": gain(ks[13], (D_MODEL,)),
    }

def reference(x, attn_norm, w_in, b_gate, sb_w_out, ret_norm, ret_w_out, w_o,
              ffn_norm, w_up, conv_w, conv_b, w_down, final_norm):
    for l in range(DEPTH):
        x = x + hybrid_mixer(x, attn_norm[l], w_in[l], b_gate[l], sb_w_out[l],
                             ret_norm[l], ret_w_out[l], w_o[l]).astype(x.dtype)
        x = x + conv_ffn(x, ffn_norm[l], w_up[l], conv_w[l], conv_b[l], w_down[l]).astype(x.dtype)
    return rms_norm(x, final_norm)


_drawn_inputs = setup_inputs


def setup_inputs(seed=0):
    import zlib

    import numpy as np

    out = dict(_drawn_inputs(seed))
    spreads = {}
    factors = {'b_gate': 8.0, 'ret_norm': 5.769, 'ffn_norm': 2.809, 'conv_b': 3.518, 'final_norm': 2.749}
    for name, (base, spread) in spreads.items():
        noise = np.random.default_rng([zlib.crc32(name.encode()), seed]).standard_normal(out[name].shape)
        drawn = base * np.exp(spread * noise) if base else spread * noise
        out[name] = __import__('jax').numpy.asarray(drawn.astype(out[name].dtype))
    for name, factor in factors.items():
        out[name] = (out[name] * factor).astype(out[name].dtype)
    return out
```

```python
from contextlib import ExitStack

import concourse.bass as bass
from concourse import mybir

ALU = mybir.AluOpType
ACT = mybir.ActivationFunctionType
F32 = mybir.dt.float32
F32R = mybir.dt.float32r
BF16 = mybir.dt.bfloat16

P = 128
S = 512
D = 1024
DEPTH = 2
KT = D // P
TT = S // P
SB_HEADS = 8
SB_PAIRS = SB_HEADS // 2
RET_HEADS = 4
FT = 22
EPS = 1e-6
NEG = -1e30

RING = 4
SLAB = 1024
AHEAD = 3
V_SLABS = 12
IN_UNITS = 20
YA0 = V_SLABS + 2 * IN_UNITS
YB0 = YA0 + 4
WO0 = YB0 + 8
UP0 = WO0 + 8
DOWN0 = UP0 + 2 * FT
SLABS = DOWN0 + FT
SLOT_USES = [(SLABS - s + RING - 1) // RING for s in range(RING)]
WO_TILE = 2 * (IN_UNITS + 8)
UP_TILE = WO_TILE + 8
DOWN_TILE = UP_TILE + 2 * FT
TILES = DOWN_TILE + 8
TILE_CREDIT = 8
SLOT_CREDIT = RING

PAR_ATTN, PAR_FFN, PAR_RET, PAR_BG, PAR_CONV = 0, 8, 16, 24, 40
NPAR = PAR_CONV + 4 * FT
BLK = {0: 0, 1: 512, 3: 896, 2: 1024}
WIDTH = {c: S - P * c for c in range(TT)}
ECOLS = 1280

QK_AT = {17 + 3 * h: h for h in range(SB_HEADS)}
TRI_AT = {19 + 3 * h: h for h in range(SB_HEADS)}
PV_AT = {20 + 3 * h: h for h in range(SB_HEADS)}
RA_AT = {42 + 3 * r: r for r in range(RET_HEADS)}
RB_AT = {43 + 3 * r: r for r in range(RET_HEADS)}
RC_AT = {44 + 3 * r: r for r in range(RET_HEADS)}
RT_AT = {45 + 3 * r: r for r in range(RET_HEADS)}
NORM1_AT = 3
GR_TILE, GATE_TILE = 16, 24
SILU_AT = 42
SIGMOID_AT = {46: range(0, 10), 51: range(10, 16)}
DVE_OUT = 6
EARLY = 2


def unit_at(i):
    if V_SLABS <= i < YA0 and (i - V_SLABS) % 2 == 1:
        j = (i - V_SLABS) // 2
        for kind, first, n in (("qk", 0, 4), ("rot", 4, 4), ("gr", 8, 4), ("gate", 12, 8)):
            if first <= j < first + n:
                return kind, j - first, j
    if YA0 <= i < YB0:
        return "ya", i - YA0, IN_UNITS + i - YA0
    if YB0 <= i < WO0 and (i - YB0) % 2 == 1:
        return "yb", (i - YB0) // 2, IN_UNITS + 4 + (i - YB0) // 2
    if WO0 <= i < UP0 and (i - WO0) % 2 == 1:
        return "wo", (i - WO0) // 2, IN_UNITS + 8 + (i - WO0) // 2
    return None


def trunk(nc, xt, wts, par, consts, rope, decay, out):
    with ExitStack() as ctx:
        def sem(name):
            return ctx.enter_context(nc.semaphore(name))

        at = [(nc.sbuf_base + 31) // 32 * 32]

        def sb(name, shape, dt, where=None):
            n = 1
            for s in shape[1:]:
                n *= s
            size = n * (2 if dt == BF16 else 4)
            if where is None:
                where = at[0]
                at[0] += (size + 31) // 32 * 32
            return nc.alloc_sbuf_tensor_at(name, shape, dt, offset=where)

        K = 1024
        x = sb("x", [P, KT, S], F32)
        u_hi = sb("u_hi", [P, KT, S], F32R)
        u_lo = sb("u_lo", [P, KT, S], F32R)
        w_hi = sb("w_hi", [P, RING, SLAB], F32R)
        ring_at = at[0]
        w_raw = sb("w_raw", [P, RING, SLAB], F32)
        w_lo = sb("w_lo", [P, RING, SLAB], F32R, ring_at)
        rinv = sb("rinv", [P, S], F32)
        pars = sb("pars", [P, DEPTH * NPAR + KT], F32)
        cst = sb("cst", [P, 3, P], F32)
        idf, onesf, halff = cst[:, 0, :], cst[:, 1, :], cst[:, 2, 0:TT]
        epsw = cst[:, 2, TT:2 * TT]
        epsf = cst[:, 2, TT:TT + 1]
        tri = sb("tri", [P, P], F32R)
        neg1 = sb("neg1", [P, P], F32R)
        idb = sb("idb", [P, P], BF16)
        negb = sb("negb", [P, P], BF16)
        rcol = sb("rcol", [P, TT], F32)
        stats = sb("stats", [P, TT, 6], F32)
        scratch = sb("scratch", [P, TT], F32)
        mv = sb("mv", [P, TT, 2], F32)
        rstd = sb("rstd", [P, 2, TT], F32)
        M = at[0]
        QK, VS, RQK, VR_, SG_, G_ = M, M + 16 * K, M + 32 * K, M + 48 * K, M + 64 * K, M + 80 * K
        TMP = M + 112 * K
        qk_hi = sb("qk_hi", [P, 2, SB_PAIRS, S], F32R, QK)
        qk_lo = sb("qk_lo", [P, SB_PAIRS, 2, S], F32R, G_)
        qk_tmp = sb("qk_tmp", [P, 2, S], F32, SG_ + 8 * K)
        osb_hi = sb("osb_hi", [P, SB_PAIRS, S], F32R, QK)
        osb_lo = sb("osb_lo", [P, SB_PAIRS, S], F32R, QK + 8 * K)
        v_hi = sb("v_hi", [P, TT, S], F32R, VS)
        v_lo = sb("v_lo", [P, TT, S], F32R, VS + 8 * K)
        dec = sb("dec", [P, RET_HEADS, S], F32, VS)
        qk_r = sb("qk_r", [P, RET_HEADS, 2, S], F32, RQK)
        or_hi = sb("or_hi", [P, KT, S], F32R, RQK)
        v_r = sb("v_r", [P, RET_HEADS, TT, 256], F32, VR_)
        or_lo = sb("or_lo", [P, KT, S], F32R, VR_)
        sg = sb("sg", [P, KT, S], F32, SG_)
        cs = sb("cs", [P, 2, S], F32, SG_)
        rtmp = sb("rtmp", [P, 2, S], F32, SG_ + 4 * K)
        gate = sb("gate", [P, 2 * KT, S], F32, G_)
        m_lo = sb("m_lo", [P, KT, S], F32R, G_)
        m_hi = sb("m_hi", [P, KT, S], F32R, G_ + 16 * K)
        sp_hi = sb("sp_hi", [P, ECOLS], F32R, G_ + 22 * K)
        sp_lo = sb("sp_lo", [P, ECOLS], F32R, G_ + 27 * K)
        att = sb("att", [P, ECOLS], F32, TMP)
        ynorm = sb("ynorm", [P, TT, 256], F32, TMP + 5 * K)
        g_hi = sb("g_hi", [P, FT, S], F32R, M)
        g_lo = sb("g_lo", [P, FT, S], F32R, M + 44 * K)
        ca = sb("ca", [P, 2, S + 8], F32, M + 88 * K)
        cb_at = M + 88 * K + 8 * (S + 8)
        cb = sb("cb", [P, 2, S], F32, cb_at)
        cc = sb("cc", [P, 2, S], F32, cb_at + 4 * K)
        sq = sb("sq", [P, S], F32, TMP)
        ssum = sb("ssum", [P, S], F32, TMP + 2 * K)
        assert TMP + 9 * K <= nc.sbuf_usable_end, (TMP + 9 * K, nc.sbuf_usable_end)
        ps = ctx.enter_context(nc.psum_tensor("ps", [P, 8, 512], F32))
        psf = ps[:, :, :].rearrange("p b n -> p (b n)")
        E0 = 4 * 512

        s_x = [sem(f"s_x{k}") for k in range(KT)]
        s_par = sem("s_par")
        s_cst = sem("s_cst")
        s_dec = sem("s_dec")
        s_cc = sem("s_cc")
        s_land = [sem(f"s_land{s}") for s in range(RING)]
        s_hi = sem("s_hi")
        s_lo = sem("s_lo")
        s_free = sem("s_free")
        s_blank = sem("s_blank")
        s_part = sem("s_part")
        s_tile = sem("s_tile")
        s_vt = sem("s_vt")
        s_sq = sem("s_sq")
        s_nrm = sem("s_nrm")
        s_rt = sem("s_rt")
        s_r = sem("s_r")
        s_uh = sem("s_uh")
        s_ul = sem("s_ul")
        s_cs = sem("s_cs")
        s_csr = sem("s_csr")
        s_rot = sem("s_rot")
        s_qh = sem("s_qh")
        s_ql = sem("s_ql")
        s_vl = sem("s_vl")
        s_ah = sem("s_ah")
        s_al = sem("s_al")
        s_qk = sem("s_qk")
        s_abs = sem("s_abs")
        s_ln = sem("s_ln")
        s_sp = sem("s_sp")
        s_sph = sem("s_sph")
        s_spl = sem("s_spl")
        s_tri = sem("s_tri")
        s_a = sem("s_a")
        s_pv = sem("s_pv")
        s_oh = sem("s_oh")
        s_ol = sem("s_ol")
        s_s = sem("s_s")
        s_sd = sem("s_sd")
        s_o = sem("s_o")
        s_bn = sem("s_bn")
        s_rs = sem("s_rs")
        s_y = sem("s_y")
        s_t = sem("s_t")
        s_gr = sem("s_gr")
        s_of = sem("s_of")
        s_orh = sem("s_orh")
        s_orl = sem("s_orl")
        s_gate = sem("s_gate")
        s_m = sem("s_m")
        s_mh = sem("s_mh")
        s_ml = sem("s_ml")
        s_zero = sem("s_zero")
        s_c1 = sem("s_c1")
        s_cv = sem("s_cv")
        s_c2 = sem("s_c2")
        s_gf = sem("s_gf")
        s_gh = sem("s_gh")
        s_gl = sem("s_gl")
        s_fsq = sem("s_fsq")
        s_gx = sem("s_gx")
        s_fin = sem("s_fin")
        s_finp = sem("s_finp")
        s_out = sem("s_out")
        s_outp = sem("s_outp")

        def pcol(l, c):
            return pars[:, bass.ds(l * NPAR + c, 1)]

        block = ctx.enter_context(nc.Block())

        @block.sync
        def _(sp):

            def load(l, slot, i):
                sp.dma_start(w_raw[:, slot, :], wts[bass.ds(l * SLABS + i, 1), :, :]
                             .rearrange("a p n -> (a p) n")).then_inc(s_land[slot], 16)

            for k in range(EARLY):
                sp.dma_start(x[:, k, :], xt[:, k, :]).then_inc(s_x[k], 16)
            with sp.Fori(0, DEPTH) as l:
                for i, need in enumerate((3, 4, 1, 2)):
                    if i == 1:
                        sp.wait_ge(s_x[EARLY - 1], 16)
                    sp.wait_ge(s_free, l * SLABS + need)
                    load(l, i, i)
                with sp.Fori(1, SLABS // RING) as r:
                    for j in range(RING):
                        sp.wait_ge(s_free, l * SLABS + r * RING + j + 1)
                        load(l, j, r * RING + j)
                for i in range(SLABS // RING * RING, SLABS):
                    sp.wait_ge(s_free, l * SLABS + i + 1)
                    load(l, i % RING, i)
            for k in range(DVE_OUT):
                sp.wait_ge(s_fin, k + 1)
                sp.dma_start(out[k], gate[:, k, :]).then_inc(s_out, 16)
            sp.wait_ge(s_out, 16 * DVE_OUT)

        @block.gpsimd
        def _(pool):
            def sum_squares(count, tile_of, tiles=KT):
                for k in range(tiles):
                    pool.wait_ge(s_x[k], 16)
                    pool.wait_ge(s_tile, tile_of(k))
                    dst = ssum if k == 0 else sq
                    if k > 0:
                        pool.wait_ge(s_sq, count + 2 * k - 1)
                    nc.gpsimd.tensor_tensor(dst[:], x[:, k, :], x[:, k, :], ALU.mult).then_inc(s_sq, 1)
                    if k > 0:
                        pool.wait_ge(s_sq, count + 2 * k)
                        nc.gpsimd.tensor_tensor(ssum[:], ssum[:], sq[:], ALU.add).then_inc(s_sq, 1)

            pool.dma_start(cst[:], consts[:, 0:3, :]).then_inc(s_cst, 16)
            pool.dma_start(gate[:, 0, 0:2 * P].rearrange("p (a b) -> p a b", a=2), consts[:, 3:5, :]).then_inc(s_cst, 16)
            pool.wait_ge(s_par, 16)
            for k in range(EARLY + 1, KT):
                pool.dma_start(x[:, k, :], xt[:, k, :]).then_inc(s_x[k], 16)
            pool.wait_ge(s_cst, 32)
            nc.gpsimd.tensor_copy(tri[:], gate[:, 0, 0:P]).then_inc(s_cc, 1)
            nc.gpsimd.tensor_scalar(neg1[:], onesf, -1.0, None, ALU.mult).then_inc(s_cc, 1)
            nc.gpsimd.tensor_copy(negb[:], gate[:, 0, P:2 * P]).then_inc(s_cc, 1)
            nc.gpsimd.tensor_copy(idb[:], idf).then_inc(s_cc, 1)
            with pool.Fori(0, DEPTH) as l:
                sum_squares(l * 30, lambda k: l * TILES + k + 1)
                for r in range(RET_HEADS):
                    n = 4 * 2 * r + 8
                    pool.wait_ge(s_bn, l * 32 + n)
                    nc.gpsimd.tensor_tensor(rstd[:, 0, :], mv[:, :, 1], epsw, ALU.add).then_inc(s_rs, 1)
                    pool.wait_ge(s_rs, l * 8 + 2 * r + 1)
                    nc.gpsimd.tensor_tensor(rstd[:, 1, :], rstd[:, 0, :], halff, ALU.pow).then_inc(s_rs, 1)
                sum_squares(l * 30 + 15, lambda k: l * TILES + TILE_CREDIT + WO_TILE + k + 1)
            sum_squares(DEPTH * 30, lambda k: DEPTH * TILES + k + 1, 4)
            for k in (4, 5):
                pool.wait_ge(s_fsq, k - 3)
                pool.wait_ge(s_sq, DEPTH * 30 + 3 + k)
                nc.gpsimd.tensor_tensor(ssum[:], ssum[:], gate[:, KT + k, :], ALU.add).then_inc(s_sq, 1)
            pool.wait_ge(s_gx, KT - DVE_OUT)
            pool.wait_ge(s_r, DEPTH * 3 + 1)
            for k in range(DVE_OUT, KT):
                nc.gpsimd.tensor_tensor(gate[:, k, :], gate[:, k, :], rinv[:], ALU.mult).then_inc(s_finp, 1)
            for k in range(DVE_OUT, KT):
                pool.wait_ge(s_finp, k - DVE_OUT + 1)
                pool.dma_start(out[k], gate[:, k, :]).then_inc(s_outp, 16)
            pool.wait_ge(s_outp, 16 * (KT - DVE_OUT))

        @block.scalar
        def _(act):
            def split_hi(l, i, g=0):
                s = i % RING
                act.wait_ge(s_land[s], l * (16 * SLOT_USES[s]) + g * 16 + 16 * (i // RING + 1))
                nc.scalar.activation(w_hi[:, s, :], w_raw[:, s, :], ACT.Copy).then_inc(s_hi, 1)

            def slab_done(l, i, g=0):
                act.wait_ge(s_free, l * SLABS + g * 4 + (i + 1 + SLOT_CREDIT))

            def root(l, n):
                act.wait_ge(s_cst, 32)
                act.wait_ge(s_nrm, l * 3 + n + 1)
                if n == 0:
                    nc.scalar.activation(rcol[:], ps[:, 2, 0:TT], ACT.Sqrt, bias=epsf, scale=1.0 / D).then_inc(s_rt, 1)
                else:
                    nc.scalar.activation(rinv[:], ps[:, 3 if n == 1 else 4, :], ACT.Sqrt, bias=epsf,
                                         scale=1.0 / D).then_inc(s_rt, 1)

            act.dma_start(pars[:], par).then_inc(s_par, 16)
            act.wait_ge(s_par, 16)

            def u_high(k, gain):
                nc.scalar.activation(u_hi[:, k, :], x[:, k, :], ACT.Copy, scale=gain).then_inc(s_uh, 1)

            for k in range(EARLY):
                act.wait_ge(s_x[k], 16)
                u_high(k, pars[:, PAR_ATTN + k:PAR_ATTN + k + 1])
            act.dma_start(x[:, EARLY, :], xt[:, EARLY, :]).then_inc(s_x[EARLY], 16)
            with act.Fori(0, DEPTH) as l:
                split_hi(l, 0)
                for k in range(EARLY, KT):
                    act.wait_ge(s_x[k], 16)
                    act.wait_ge(s_tile, l * TILES + k + 1)
                    u_high(k, pcol(l, PAR_ATTN + k))
                    if k - EARLY + 1 < AHEAD:
                        split_hi(l, k - EARLY + 1)
                act.dma_start(cs[:], rope).then_inc(s_cs, 16)
                for i in range(UP0):
                    if i == NORM1_AT:
                        root(l, 0)
                        root(l, 1)
                    if i in (3, 7, 11):
                        g = i // 4
                        slab_done(l, i)
                        if g == 0:
                            act.wait_ge(s_r, l * 3 + 1)
                        for tt in range(TT):
                            bank = (0 if g == 1 else 4) + tt
                            if g == 0:
                                dst, src = v_hi[:, tt, :], ps[:, bank, :]
                            else:
                                dst = v_r[:, 2 * g - 2:2 * g, tt, :]
                                src = ps[:, bank, :].rearrange("p (h e) -> p h e", h=2)
                            nc.scalar.activation(dst, src, ACT.Copy, scale=rcol[:, tt:tt + 1]).then_inc(s_vt, 1)
                    if i in TRI_AT:
                        h = TRI_AT[i]
                        act.wait_ge(s_tri, l * 8 + h + 1)
                        nc.scalar.activation(att[:], psf[:, E0:E0 + ECOLS], ACT.Exp).then_inc(s_a, 1)
                        act.wait_ge(s_a, l * 8 + h + 1)
                        nc.scalar.activation(sp_hi[:], att[:], ACT.Copy).then_inc(s_ah, 1)
                    if i in PV_AT:
                        h = PV_AT[i]
                        b, p = 64 * (h % 2), h // 2
                        act.wait_ge(s_pv, l * 8 + h + 1)
                        nc.scalar.activation(osb_hi[b:b + 64, p, :], ps[b:b + 64, 7, :], ACT.Copy).then_inc(s_oh, 1)
                        if h == SB_HEADS - 1:
                            act.dma_start(dec[:], decay).then_inc(s_dec, 16)
                    if i in RT_AT:
                        r = RT_AT[i]
                        for e in range(2):
                            act.wait_ge(s_of, l * 8 + 2 * r + e + 1 + 1)
                            nc.scalar.activation(or_hi[:, 2 * r + e, :], sg[:, 2 * r + e, :], ACT.Copy).then_inc(s_orh, 1)
                    u = unit_at(i)
                    if u:
                        kind, j, n = u
                        for t in range(2):
                            if kind == "qk":
                                act.wait_ge(s_tile, l * TILES + TILE_CREDIT + 2 * n + t + 1)
                                nc.scalar.activation(qk_hi[:, j % 2, 2 * (j // 2) + t, :], qk_tmp[:, t, :], ACT.Copy).then_inc(s_qh, 1)
                            if kind == "yb":
                                act.wait_ge(s_m, l * 8 + 2 * j + t + 1)
                                nc.scalar.activation(m_hi[:, 2 * j + t, :], gate[:, 2 * j + t, :], ACT.Copy).then_inc(s_mh, 1)
                            if kind == "wo":
                                act.wait_ge(s_tile, l * TILES + TILE_CREDIT + 2 * n + t + 1)
                                u_high(2 * j + t, pcol(l, PAR_FFN + 2 * j + t))
                    if i in QK_AT:
                        h = QK_AT[i]
                        act.wait_ge(s_qk, l * 8 + h + 1)
                        nc.scalar.activation(att[:], psf[:, E0:E0 + ECOLS], ACT.Abs).then_inc(s_abs, 1)
                        act.wait_ge(s_abs, l * 8 + h + 1)
                        nc.scalar.activation(att[:], att[:], ACT.Exp, scale=-1.0).then_inc(s_ln, 1)
                        act.wait_ge(s_ln, l * 16 + 2 * h + 1)
                        nc.scalar.activation(att[:], att[:], ACT.Ln, bias=1.0).then_inc(s_ln, 1)
                    if i == SILU_AT:
                        for k in range(KT):
                            act.wait_ge(s_tile, l * TILES + TILE_CREDIT + GR_TILE + k + 1)
                            nc.scalar.activation(sg[:, k, :], sg[:, k, :], ACT.Silu).then_inc(s_gr, 1)
                    if i in SIGMOID_AT:
                        for k in SIGMOID_AT[i]:
                            act.wait_ge(s_tile, l * TILES + TILE_CREDIT + GATE_TILE + k + 1)
                            nc.scalar.activation(gate[:, k, :], gate[:, k, :], ACT.Sigmoid,
                                                 bias=pcol(l, PAR_BG + k)).then_inc(s_gate, 1)
                    if i in QK_AT:
                        act.wait_ge(s_sp, l * 8 + QK_AT[i] + 1)
                        nc.scalar.activation(sp_hi[:], att[:], ACT.Copy).then_inc(s_sph, 1)
                    split_hi(l, i + AHEAD)
                root(l, 2)
                with act.Fori(0, FT // 2) as g:
                    for j in range(4):
                        split_hi(l, UP0 + j + AHEAD, g)
                        if j % 2 == 1:
                            h = j // 2
                            n = UP_TILE + 2 * h
                            act.wait_ge(s_tile, l * TILES + g * 4 + (TILE_CREDIT + n + 1))
                            f = g * 2 + h
                            nc.scalar.activation(cc[:, h, :], ca[:, h, 2:2 + S], ACT.Identity,
                                                 scale=pars[:, bass.ds(l * NPAR + g * 8 + (PAR_CONV + 4 * h + 2), 1)],
                                                 bias=pars[:, bass.ds(l * NPAR + g * 8 + (PAR_CONV + 4 * h + 3), 1)]).then_inc(s_c1, 1)
                            act.wait_ge(s_cv, l * (2 * FT) + g * 4 + (2 * h + 2))
                            nc.scalar.activation(cc[:, h, :], cc[:, h, :], ACT.Silu).then_inc(s_c2, 1)
                            act.wait_ge(s_gf, l * FT + g * 2 + (h + 1))
                            nc.scalar.activation(g_hi[:, bass.ds(f, 1), :], cb[:, h:h + 1, :], ACT.Copy).then_inc(s_gh, 1)
                for i in range(DOWN0, SLABS):
                    if i + AHEAD < SLABS:
                        split_hi(l, i + AHEAD)
                    if i == DOWN0 + 10:
                        for k in range(EARLY):
                            act.wait_ge(s_tile, l * TILES + TILE_CREDIT + DOWN_TILE + k + 1)
                            u_high(k, pcol(l + 1, PAR_ATTN + k))
            for k in range(4, KT):
                act.wait_ge(s_tile, DEPTH * TILES + k + 1)
                nc.scalar.activation(gate[:, KT + k, :], x[:, k, :], ACT.Square).then_inc(s_fsq, 1)
            act.wait_ge(s_nrm, DEPTH * 3 + 1)
            nc.scalar.activation(rinv[:], ps[:, 4, :], ACT.Sqrt, bias=epsf, scale=1.0 / D).then_inc(s_rt, 1)

        @block.vector
        def _(dve):
            def split_lo(l, i, g=0):
                s = i % RING
                dve.wait_ge(s_hi, l * SLABS + g * 4 + (i + 1))
                nc.vector.tensor_tensor(w_lo[:, s, :], w_raw[:, s, :], w_hi[:, s, :].bitcast(F32), ALU.subtract).then_inc(s_lo, 1)

            def slab_done(l, i, g=0):
                dve.wait_ge(s_free, l * SLABS + g * 4 + (i + 1 + SLOT_CREDIT))

            def u_low(count, k, gain):
                dve.wait_ge(s_uh, count + k + 1)
                nc.vector.scalar_tensor_tensor(out=u_lo[:, k, :], in0=x[:, k, :], scalar=gain, in1=u_hi[:, k, :].bitcast(F32),
                                               op0=ALU.mult, op1=ALU.subtract).then_inc(s_ul, 1)

            def last_tile(l):
                dve.wait_ge(s_blank, 1)
                dve.wait_ge(s_free, l * SLABS + SLOT_CREDIT)
                nc.vector.tensor_tensor(x[:, KT - 1, :], x[:, KT - 1, :], ps[:, 3, :], ALU.add).then_inc(s_tile, 1)

            nc.vector.sem_inc(s_tile, TILE_CREDIT - 1)
            nc.vector.sem_inc(s_ol, 1)
            nc.vector.sem_inc(s_of, 1)
            nc.vector.sem_inc(s_gl, 1)
            nc.vector.memset(ps[:, 3, :], 0.0).then_inc(s_blank, 1)
            dve.wait_ge(s_par, 16)
            for k in range(EARLY):
                dve.wait_ge(s_x[k], 16)
                u_low(0, k, pars[:, PAR_ATTN + k:PAR_ATTN + k + 1])
            with dve.Fori(0, DEPTH) as l:
                split_lo(l, 0)
                for k in range(EARLY, KT):
                    dve.wait_ge(s_x[k], 16)
                    if k == KT - 1:
                        last_tile(l)
                    u_low(l * 16, k, pcol(l, PAR_ATTN + k))
                    if k - EARLY + 1 < AHEAD:
                        split_lo(l, k - EARLY + 1)
                for i in range(UP0):
                    if i == NORM1_AT:
                        dve.wait_ge(s_rt, l * 3 + 1)
                        nc.vector.reciprocal(rcol[:], rcol[:]).then_inc(s_r, 1)
                        dve.wait_ge(s_rt, l * 3 + 2)
                        nc.vector.reciprocal(rinv[:], rinv[:]).then_inc(s_r, 1)
                        dve.wait_ge(s_r, l * 3 + 2)
                        dve.wait_ge(s_cs, l * 16 + 16)
                        for a in range(2):
                            nc.vector.tensor_tensor(cs[:, a, :], cs[:, a, :], rinv[:], ALU.mult).then_inc(s_csr, 1)
                    if i == 3:
                        for tt in range(TT):
                            dve.wait_ge(s_vt, l * 12 + tt + 1)
                            nc.vector.scalar_tensor_tensor(out=v_lo[:, tt, :], in0=ps[:, 4 + tt, :], scalar=rcol[:, tt:tt + 1],
                                                           in1=v_hi[:, tt, :].bitcast(F32), op0=ALU.mult,
                                                           op1=ALU.subtract).then_inc(s_vl, 1)
                    if i in TRI_AT:
                        dve.wait_ge(s_ah, l * 8 + TRI_AT[i] + 1)
                        nc.vector.tensor_tensor(sp_lo[:], att[:], sp_hi[:].bitcast(F32), ALU.subtract).then_inc(s_al, 1)
                    if i in PV_AT:
                        h = PV_AT[i]
                        b, p = 64 * (h % 2), h // 2
                        dve.wait_ge(s_oh, l * 8 + h + 1)
                        nc.vector.tensor_tensor(osb_lo[b:b + 64, p, :], ps[b:b + 64, 7, :],
                                                osb_hi[b:b + 64, p, :].bitcast(F32), ALU.subtract).then_inc(s_ol, 1)
                    if i in RT_AT:
                        r = RT_AT[i]
                        dve.wait_ge(s_t, l * 4 + r + 1)
                        dve.wait_ge(s_gr, l * 8 + 8)
                        for e in range(2):
                            k = 2 * r + e
                            nc.vector.scalar_tensor_tensor(out=sg[:, k, :], in0=ps[:, 6 + e, :], scalar=pcol(l, PAR_RET + k),
                                                           in1=sg[:, k, :], op0=ALU.mult, op1=ALU.mult).then_inc(s_of, 1)
                        for e in range(2):
                            k = 2 * r + e
                            dve.wait_ge(s_orh, l * 8 + k + 1)
                            nc.vector.tensor_tensor(or_lo[:, k, :], sg[:, k, :], or_hi[:, k, :].bitcast(F32),
                                                    ALU.subtract).then_inc(s_orl, 1)
                    for where, blocks in ((RA_AT, (0, 1)), (RB_AT, (2, 3))):
                        if i in where:
                            r = where[i]
                            for c in blocks:
                                dve.wait_ge(s_dec, l * 16 + 16)
                                dve.wait_ge(s_s, l * 16 + 4 * r + c + 1)
                                nc.vector.tensor_tensor(att[:, BLK[c]:BLK[c] + WIDTH[c]], ps[:, 4 + c % 2, 0:WIDTH[c]],
                                                        dec[:, r, 0:WIDTH[c]], ALU.mult).then_inc(s_sd, 1)
                    if i in RC_AT:
                        r = RC_AT[i]
                        dve.wait_ge(s_o, l * 4 + r + 1)
                        for j in range(TT):
                            nc.vector.bn_stats(stats[:, j, :], ps[:, 6 + j // 2, (j % 2) * 256:(j % 2) * 256 + 256]).then_inc(s_bn, 1)
                        dve.wait_ge(s_bn, l * 32 + 8 * r + 4)
                        nc.vector.tensor_copy(scratch[:], stats[:, :, 0])
                        for j in range(TT):
                            nc.vector.bn_aggr(mv[:, j, :], stats[:, j, :]).then_inc(s_bn, 1)
                        dve.wait_ge(s_rs, l * 8 + 2 * r + 2)
                        for j in range(TT):
                            nc.vector.tensor_scalar(ynorm[:, j, :], ps[:, 6 + j // 2, (j % 2) * 256:(j % 2) * 256 + 256],
                                                    mv[:, j, 0:1], rstd[:, 1, j:j + 1], ALU.subtract, ALU.mult).then_inc(s_y, 1)
                    u = unit_at(i)
                    if u:
                        kind, j, n = u
                        if i == UP0 - 1:
                            dve.wait_ge(s_part, l * 4 + 1)
                        else:
                            slab_done(l, i)
                        for t in range(2):
                            src = ps[:, 2 * (n % 2) + t, :]
                            k = 2 * j + t
                            if kind == "qk":
                                which, p = j % 2, 2 * (j // 2) + t
                                dve.wait_ge(s_r, l * 3 + 2)
                                if j > 0:
                                    dve.wait_ge(s_ql, l * 8 + 2 * (j - 1) + t + 1)
                                nc.vector.scalar_tensor_tensor(out=qk_tmp[:, t, :], in0=src, scalar=(0.125, 1.0)[which],
                                                               in1=rinv[:], op0=ALU.mult, op1=ALU.mult).then_inc(s_tile, 1)
                            if kind == "rot":
                                which, h = j // 2, 2 * (j % 2) + t
                                step = l * 24 + 3 * k
                                dve.wait_ge(s_csr, l * 2 + 2)
                                if k >= 2:
                                    dve.wait_ge(s_rot, step - 3)
                                nc.vector.tensor_tensor(qk_r[:, h, which, :], src, cs[:, 0, :], ALU.mult).then_inc(s_rot, 1)
                                nc.vector.tensor_tensor(rtmp[0:64, t, :], ps[64:128, 2 * (n % 2) + t, :], cs[64:128, 1, :],
                                                        ALU.mult).then_inc(s_rot, 1)
                                nc.vector.tensor_tensor(rtmp[64:128, t, :], ps[0:64, 2 * (n % 2) + t, :], cs[0:64, 1, :],
                                                        ALU.mult).then_inc(s_tile, 1)
                                dve.wait_ge(s_rot, step + 2)
                                dve.wait_ge(s_tile, l * TILES + TILE_CREDIT + 2 * n + t + 1)
                                nc.vector.tensor_tensor(qk_r[:, h, which, :], qk_r[:, h, which, :], rtmp[:, t, :], ALU.add).then_inc(s_rot, 1)
                            if kind in ("gr", "gate"):
                                dst = sg if kind == "gr" else gate
                                nc.vector.tensor_tensor(dst[:, k, :], src, rinv[:], ALU.mult).then_inc(s_tile, 1)
                            if kind == "ya":
                                dve.wait_ge(s_gate, l * 16 + k + 1)
                                nc.vector.tensor_tensor(gate[:, k, :], gate[:, k, :], src, ALU.mult).then_inc(s_tile, 1)
                            if kind == "yb":
                                dve.wait_ge(s_gate, l * 16 + 8 + k + 1)
                                nc.vector.tensor_tensor(gate[:, 8 + k, :], gate[:, 8 + k, :], src, ALU.mult).then_inc(s_tile, 1)
                                dve.wait_ge(s_tile, l * TILES + TILE_CREDIT + 2 * n + t + 1)
                                nc.vector.tensor_tensor(gate[:, k, :], gate[:, k, :], gate[:, 8 + k, :], ALU.add).then_inc(s_m, 1)
                            if kind == "wo":
                                if i == UP0 - 1 and t == 1:
                                    slab_done(l, i)
                                nc.vector.tensor_tensor(x[:, k, :], x[:, k, :], src, ALU.add).then_inc(s_tile, 1)
                        if kind == "qk":
                            for t in range(2):
                                which, p = j % 2, 2 * (j // 2) + t
                                dve.wait_ge(s_qh, l * 8 + 2 * j + t + 1)
                                nc.vector.tensor_tensor(qk_lo[:, p, which, :], qk_tmp[:, t, :], qk_hi[:, which, p, :].bitcast(F32),
                                                        ALU.subtract).then_inc(s_ql, 1)
                        if kind == "yb":
                            for t in range(2):
                                k = 2 * j + t
                                dve.wait_ge(s_mh, l * 8 + k + 1)
                                nc.vector.tensor_tensor(m_lo[:, k, :], gate[:, k, :], m_hi[:, k, :].bitcast(F32),
                                                        ALU.subtract).then_inc(s_ml, 1)
                        if kind == "wo":
                            for t in range(2):
                                u_low(l * 16 + 8, 2 * j + t, pcol(l, PAR_FFN + 2 * j + t))
                    if i in QK_AT:
                        h = QK_AT[i]
                        dve.wait_ge(s_ln, l * 16 + 2 * h + 2)
                        nc.vector.scalar_tensor_tensor(out=att[:], in0=psf[:, E0:E0 + ECOLS], scalar=0.0, in1=att[:],
                                                       op0=ALU.max, op1=ALU.add).then_inc(s_sp, 1)
                        dve.wait_ge(s_sph, l * 8 + h + 1)
                        nc.vector.tensor_tensor(sp_lo[:], att[:], sp_hi[:].bitcast(F32), ALU.subtract).then_inc(s_spl, 1)
                    split_lo(l, i + AHEAD)
                nc.vector.memset(ca[:, :, 0:2], 0.0).then_inc(s_zero, 1)
                dve.wait_ge(s_zero, l + 1)
                dve.wait_ge(s_rt, l * 3 + 3)
                nc.vector.reciprocal(rinv[:], rinv[:]).then_inc(s_r, 1)
                with dve.Fori(0, FT // 2) as g:
                    for j in range(4):
                        split_lo(l, UP0 + j + AHEAD, g)
                        if j % 2 == 1:
                            h = j // 2
                            slab_done(l, UP0 + j, g)
                            cw = [pars[:, bass.ds(l * NPAR + g * 8 + (PAR_CONV + 4 * h + c), 1)] for c in range(2)]
                            dve.wait_ge(s_r, l * 3 + 3)
                            nc.vector.tensor_tensor(ca[:, h, 2:2 + S], ps[:, 2 * h, :], rinv[:], ALU.mult).then_inc(s_tile, 1)
                            dve.wait_ge(s_gl, l * FT + g * 2 + (h + 1))
                            nc.vector.tensor_tensor(cb[:, h, :], ps[:, 2 * h + 1, :], rinv[:], ALU.mult).then_inc(s_tile, 1)
                            dve.wait_ge(s_c1, l * FT + g * 2 + (h + 1))
                            nc.vector.scalar_tensor_tensor(out=cc[:, h, :], in0=ca[:, h, 1:1 + S], scalar=cw[1], in1=cc[:, h, :],
                                                           op0=ALU.mult, op1=ALU.add).then_inc(s_cv, 1)
                            dve.wait_ge(s_cv, l * (2 * FT) + g * 4 + (2 * h + 1))
                            nc.vector.scalar_tensor_tensor(out=cc[:, h, :], in0=ca[:, h, 0:S], scalar=cw[0], in1=cc[:, h, :],
                                                           op0=ALU.mult, op1=ALU.add).then_inc(s_cv, 1)
                            dve.wait_ge(s_c2, l * FT + g * 2 + (h + 1))
                            dve.wait_ge(s_tile, l * TILES + g * 4 + (TILE_CREDIT + UP_TILE + 2 * h + 2))
                            nc.vector.tensor_tensor(cb[:, h, :], cc[:, h, :], cb[:, h, :], ALU.mult).then_inc(s_gf, 1)
                            dve.wait_ge(s_gh, l * FT + g * 2 + (h + 1))
                            nc.vector.tensor_tensor(g_lo[:, bass.ds(g * 2 + h, 1), :], cb[:, h:h + 1, :],
                                                    g_hi[:, bass.ds(g * 2 + h, 1), :].bitcast(F32), ALU.subtract).then_inc(s_gl, 1)
                for i in range(DOWN0, SLABS):
                    if i + AHEAD < SLABS:
                        split_lo(l, i + AHEAD)
                    if i in (DOWN0 + 10, SLABS - 1):
                        q = (i - DOWN0) // 11
                        for t in range(4 if q == 0 else 3):
                            if q == 1:
                                dve.wait_ge(s_part, l * 4 + 2 + t)
                            else:
                                slab_done(l, i)
                            nc.vector.tensor_tensor(x[:, 4 * q + t, :], x[:, 4 * q + t, :], ps[:, 4 - 4 * q + t, :],
                                                    ALU.add).then_inc(s_tile, 1)
                        if q == 0:
                            for t in range(EARLY):
                                u_low(l * 16 + 16, t, pcol(l + 1, PAR_ATTN + t))
            last_tile(DEPTH)
            for k in range(DVE_OUT, KT):
                dve.wait_ge(s_tile, DEPTH * TILES + k + 1)
                nc.vector.tensor_scalar(gate[:, k, :], x[:, k, :], pars[:, DEPTH * NPAR + k:DEPTH * NPAR + k + 1], None,
                                        ALU.mult).then_inc(s_gx, 1)
            dve.wait_ge(s_rt, DEPTH * 3 + 1)
            nc.vector.reciprocal(rinv[:], rinv[:]).then_inc(s_r, 1)
            dve.wait_ge(s_r, DEPTH * 3 + 1)
            for k in range(DVE_OUT):
                nc.vector.scalar_tensor_tensor(out=gate[:, k, :], in0=x[:, k, :], scalar=pars[:, DEPTH * NPAR + k:DEPTH * NPAR + k + 1],
                                               in1=rinv[:], op0=ALU.mult, op1=ALU.mult).then_inc(s_fin, 1)

        @block.tensor
        def _(pe):
            def slab_ready(l, i, g=0):
                pe.wait_ge(s_lo, l * SLABS + g * 4 + (i + 1))

            def three(dst, a_hi, a_lo, b_hi, b_lo, start, stop):
                nc.tensor.matmul(dst, a_hi, b_hi, start=start, stop=False)
                nc.tensor.matmul(dst, a_hi, b_lo, start=False, stop=False)
                return nc.tensor.matmul(dst, a_lo, b_hi, start=False, stop=stop)

            def unit_tail(slot, r_hi, r_lo, k0, pair):
                for t in range(2):
                    for kk in range(4):
                        c = kk * 256 + t * P
                        mm = three(ps[:, 2 * pair + t, :], w_hi[:, slot, c:c + P], w_lo[:, slot, c:c + P],
                                   r_hi[:, k0 + kk, :], r_lo[:, k0 + kk, :], False, kk == 3)
                    mm.then_inc(s_part if t == 0 else s_free, 1)

            def unit_slab(slot, r_hi, r_lo, k0, first, last, pair, before_k=None, before_tile=None):
                for kk in range(4):
                    if before_k:
                        before_k(k0 + kk)
                    for t in range(2):
                        if kk == 0 and first:
                            before_tile(t)
                        c = kk * 256 + t * P
                        mm = three(ps[:, 2 * pair + t, :], w_hi[:, slot, c:c + P], w_lo[:, slot, c:c + P],
                                   r_hi[:, k0 + kk, :], r_lo[:, k0 + kk, :], first and kk == 0, last and kk == 3)
                mm.then_inc(s_free, 1)

            def v_slab(slot, k0, first, last, quad, before_k, before_tile):
                for kk in range(2):
                    before_k(k0 + kk)
                    for tt in range(TT):
                        if kk == 0 and first:
                            before_tile(tt)
                        c = kk * 512
                        mm = three(ps[:, 4 * quad + tt, :], u_hi[:, k0 + kk, tt * P:(tt + 1) * P], u_lo[:, k0 + kk, tt * P:(tt + 1) * P],
                                   w_hi[:, slot, c:c + 512], w_lo[:, slot, c:c + 512], first and kk == 0, last and kk == 1)
                mm.then_inc(s_free, 1)

            def scores(l, h):
                b, p = 64 * (h % 2), h // 2
                pe.wait_ge(s_ql, l * 8 + (4 if p < 2 else 8))
                if h == 0:
                    pe.wait_ge(s_vt, l * 12 + 12)
                q_hi, k_hi = qk_hi[b:b + 64, 0, p, :], qk_hi[b:b + 64, 1, p, :]
                q_lo, k_lo = qk_lo[b:b + 64, p, 0, :], qk_lo[b:b + 64, p, 1, :]
                for c in (0, 1, 3, 2):
                    for n, (k_part, q_part) in enumerate(((k_hi, q_hi), (k_hi, q_lo), (k_lo, q_hi))):
                        nc.tensor.matmul(psf[:, E0 + BLK[c]:E0 + BLK[c] + WIDTH[c]], k_part[:, c * P:(c + 1) * P],
                                         q_part[:, c * P:S], start=(c != 3 and n == 0), stop=False, skip_group_check=True)
                for c in (0, 1, 3, 2):
                    mm = nc.tensor.matmul(psf[:, E0 + BLK[c]:E0 + BLK[c] + P], idb[:], negb[:], start=False, stop=(c != 1),
                                          skip_group_check=True)
                mm.then_inc(s_qk, 1)

            def suffix(l, h):
                pe.wait_ge(s_spl, l * 8 + h + 1)
                for c in (0, 1, 3, 2):
                    for part in (sp_hi, sp_lo):
                        for c2 in range(c, TT):
                            o = E0 + BLK[c] + (c2 - c) * P
                            mm = nc.tensor.matmul(psf[:, o:o + WIDTH[c2]], tri[:] if c2 == c else neg1[:],
                                                  part[:, BLK[c2]:BLK[c2] + WIDTH[c2]], start=False, stop=True,
                                                  skip_group_check=True)
                mm.then_inc(s_tri, 1)

            def weigh(l, h):
                p = h // 2
                pe.wait_ge(s_al, l * 8 + h + 1)
                pe.wait_ge(s_ol, l * 8 + h + 1)
                pe.wait_ge(s_vt, l * 12 + 12)
                for c in range(TT):
                    for n, (v_part, a_part) in enumerate(((v_hi, sp_hi), (v_hi, sp_lo), (v_lo, sp_hi))):
                        mm = nc.tensor.matmul(ps[:, 7, c * P:S], v_part[:, c, p * P:(p + 1) * P],
                                              a_part[:, BLK[c]:BLK[c] + WIDTH[c]], start=(c == 0 and n == 0),
                                              stop=(c == TT - 1 and n == 2), skip_group_check=True)
                mm.then_inc(s_pv, 1)

            def ret_scores(l, r, c):
                if c >= 2:
                    pe.wait_ge(s_sd, l * 16 + 4 * r + c - 1)
                nc.tensor.matmul(ps[:, 4 + c % 2, 0:WIDTH[c]], qk_r[:, r, 1, c * P:(c + 1) * P], qk_r[:, r, 0, c * P:S],
                                 start=True, stop=True).then_inc(s_s, 1)

            def ret_values(l, r, c):
                pe.wait_ge(s_sd, l * 16 + 4 * r + c + 1)
                for j in range(c, TT):
                    o = BLK[c] + (j - c) * P
                    mm = nc.tensor.matmul(ps[:, 6 + j // 2, (j % 2) * 256:(j % 2) * 256 + 256], att[:, o:o + P], v_r[:, r, c, :],
                                          start=(c == 0 and j % 2 == 0), stop=(c == j), skip_group_check=True)
                if c == TT - 1:
                    mm.then_inc(s_o, 1)

            nc.tensor.sem_inc(s_free, SLOT_CREDIT)
            with pe.Fori(0, DEPTH) as l:
                for i in range(UP0):
                    slab_ready(l, i)
                    slot = i % RING
                    if i < V_SLABS:
                        g, q = i // 4, i % 4

                        def operand(k):
                            if g == 0:
                                pe.wait_ge(s_ul, l * 16 + k + 1)

                        def bank_free(tt):
                            if g == 0:
                                pe.wait_ge(s_tile, l * TILES + tt + 1)
                            elif g == 1:
                                pe.wait_ge(s_tile, l * TILES + 4 + tt + 1)
                                if tt == 2:
                                    pe.wait_ge(s_rt, l * 3 + 1)
                                if tt == 3:
                                    pe.wait_ge(s_rt, l * 3 + 2)
                            else:
                                pe.wait_ge(s_vl, l * 4 + tt + 1)
                        v_slab(slot, 2 * q, q == 0, q == 3, 0 if g == 1 else 1, operand, bank_free)
                    elif i < YA0:
                        j, half = (i - V_SLABS) // 2, (i - V_SLABS) % 2

                        def bank_free(t):
                            if j < 2:
                                pe.wait_ge(s_vt, l * 12 + 4 + 2 * j + t + 1)
                            else:
                                pe.wait_ge(s_tile, l * TILES + TILE_CREDIT + 2 * (j - 2) + t + 1)
                        unit_slab(slot, u_hi, u_lo, 4 * half, half == 0, half == 1, j % 2, None, bank_free)
                    else:
                        base = YA0 if i < YB0 else YB0 if i < WO0 else WO0
                        r_hi, r_lo = ((osb_hi, osb_lo) if i < YB0 else (or_hi, or_lo) if i < WO0 else (m_hi, m_lo))
                        if i < YB0:
                            n, half = IN_UNITS + i - YA0, 0
                        else:
                            n = (IN_UNITS + 4 if i < WO0 else IN_UNITS + 8) + (i - base) // 2
                            half = (i - base) % 2

                        def bank_free(t):
                            pe.wait_ge(s_tile, l * TILES + TILE_CREDIT + 2 * (n - 2) + t + 1)

                        def operand(k):
                            if i < YB0:
                                pe.wait_ge(s_ol, l * 8 + 8 + 1)
                            elif i < WO0:
                                pe.wait_ge(s_orl, l * 8 + k + 1)
                            else:
                                pe.wait_ge(s_ml, l * 8 + k + 1)
                        one = i < YB0
                        if i == UP0 - 1:
                            unit_tail(slot, r_hi, r_lo, 4, n % 2)
                        else:
                            unit_slab(slot, r_hi, r_lo, 4 * half, half == 0, one or half == 1, n % 2, operand, bank_free)
                    if i == NORM1_AT:
                        pe.wait_ge(s_cst, 32)
                        pe.wait_ge(s_cc, 4)
                        pe.wait_ge(s_sq, l * 30 + 15)
                        for tt in range(TT):
                            mm = nc.tensor.matmul(ps[:, 2, tt:tt + 1], ssum[:, tt * P:(tt + 1) * P], onesf[:, 0:1],
                                                  start=True, stop=True)
                        mm.then_inc(s_nrm, 1)
                        nc.tensor.matmul(ps[:, 3, :], onesf, ssum[:], start=True, stop=True).then_inc(s_nrm, 1)
                    if i in TRI_AT:
                        suffix(l, TRI_AT[i])
                    if i in PV_AT:
                        weigh(l, PV_AT[i])
                    if i in QK_AT:
                        scores(l, QK_AT[i])
                    if i in RT_AT:
                        r = RT_AT[i]
                        pe.wait_ge(s_y, l * 16 + 4 * r + 4)
                        for e in range(2):
                            for j in range(TT):
                                mm = nc.tensor.transpose(ps[:, 6 + e, j * P:(j + 1) * P], ynorm[:, j, e * P:(e + 1) * P], idf)
                        mm.then_inc(s_t, 1)
                    if i in RA_AT:
                        r = RA_AT[i]
                        pe.wait_ge(s_rot, l * 24 + 24)
                        if r == 0:
                            pe.wait_ge(s_ol, l * 8 + 8 + 1)
                        ret_scores(l, r, 0)
                        ret_scores(l, r, 1)
                    if i in RB_AT:
                        r = RB_AT[i]
                        pe.wait_ge(s_of, l * 8 + 2 * r + 1)
                        ret_values(l, r, 0)
                        ret_scores(l, r, 2)
                        ret_values(l, r, 1)
                        ret_scores(l, r, 3)
                    if i in RC_AT:
                        r = RC_AT[i]
                        ret_values(l, r, 2)
                        ret_values(l, r, 3)
                def up_units(g, first):
                    for j in range(4):
                        slab_ready(l, UP0 + j, g)
                        h = j // 2

                        def bank_free(t):
                            pe.wait_ge(s_tile, l * TILES + g * 4 + (TILE_CREDIT + UP_TILE + 2 * (h - 2) + t + 1))

                        def operand(k):
                            if first:
                                pe.wait_ge(s_ul, l * 16 + 8 + k + 1)
                        unit_slab((UP0 + j) % RING, u_hi, u_lo, 4 * (j % 2), j % 2 == 0, j % 2 == 1, h, operand, bank_free)
                        if first and j == 0:
                            pe.wait_ge(s_sq, l * 30 + 30)
                            nc.tensor.matmul(ps[:, 4, :], onesf, ssum[:], start=True, stop=True).then_inc(s_nrm, 1)

                up_units(0, True)
                with pe.Fori(1, FT // 2) as g:
                    up_units(g, False)
                for i in range(DOWN0, SLABS):
                    slab_ready(l, i)
                    q, s = (i - DOWN0) // 11, (i - DOWN0) % 11
                    slot = i % RING
                    if i == SLABS - 1:
                        for t in range(4):
                            for kk in range(2):
                                c = kk * 512 + t * P
                                mm = three(ps[:, t, :], w_hi[:, slot, c:c + P], w_lo[:, slot, c:c + P],
                                           g_hi[:, 2 * s + kk, :], g_lo[:, 2 * s + kk, :], False, kk == 1)
                            mm.then_inc(s_part if t < 3 else s_free, 1)
                        continue
                    for kk in range(2):
                        f = 2 * s + kk
                        if q == 0:
                            pe.wait_ge(s_gl, l * FT + f + 1 + 1)
                        for t in range(4):
                            if q == 1 and f == 0:
                                pe.wait_ge(s_tile, l * TILES + TILE_CREDIT + DOWN_TILE - 4 + t + 1)
                            c = kk * 512 + t * P
                            mm = three(ps[:, 4 - 4 * q + t, :], w_hi[:, slot, c:c + P], w_lo[:, slot, c:c + P],
                                       g_hi[:, f, :], g_lo[:, f, :], f == 0, f == FT - 1)
                    mm.then_inc(s_free, 1)
            pe.wait_ge(s_sq, DEPTH * 30 + 9)
            nc.tensor.matmul(ps[:, 4, :], onesf, ssum[:], start=True, stop=False)
            for k in range(6, KT):
                pe.wait_ge(s_fsq, k - 3)
                mm = nc.tensor.matmul(ps[:, 4, :], onesf, gate[:, KT + k, :], start=False, stop=(k == KT - 1))
            mm.then_inc(s_nrm, 1)


def kernel(x, attn_norm, w_in, b_gate, sb_w_out, ret_norm, ret_w_out, w_o,
           ffn_norm, w_up, conv_w, conv_b, w_down, final_norm):
    import numpy as np
    import concourse.bacc as bacc
    from concourse.bass_utils import run_bass_kernel_spmd as run

    f32 = np.float32

    def unit_slabs(w):
        k, n = w.shape
        return w.reshape(k // 512, 4, P, n // 256, 256).transpose(3, 0, 2, 1, 4).reshape(-1, P, SLAB)

    def group_slabs(w):
        k, n = w.shape
        return w.reshape(k // 256, 2, P, n // 512, 512).transpose(3, 0, 2, 1, 4).reshape(-1, P, SLAB)

    def cols(v):
        return np.asarray(v).reshape(-1, P).T

    slabs, pars = [], []
    for l in range(DEPTH):
        w = np.asarray(w_in[l])
        q_s, k_s, v_s = w[:, 0:512], w[:, 512:1024], w[:, 1024:1536]
        q_r, k_r, v_r = w[:, 1536:2048], w[:, 2048:2560], w[:, 2560:3584]
        g_r, gates = w[:, 3584:4608], w[:, 4608:6656]
        qk = np.stack([q_s.reshape(D, 2, 256), k_s.reshape(D, 2, 256)], axis=2).reshape(D, 1024)
        up = np.asarray(w_up[l]).reshape(D, 2, FT, P).transpose(0, 2, 1, 3).reshape(D, 2 * FT * P)
        slabs += [group_slabs(v_s), group_slabs(v_r), unit_slabs(qk), unit_slabs(q_r), unit_slabs(k_r),
                  unit_slabs(g_r), unit_slabs(gates), unit_slabs(np.asarray(sb_w_out[l])),
                  unit_slabs(np.asarray(ret_w_out[l])), unit_slabs(np.asarray(w_o[l])), unit_slabs(up),
                  group_slabs(np.asarray(w_down[l]))]
        taps = np.concatenate([np.asarray(conv_w[l]), np.asarray(conv_b[l])[None]], axis=0)
        pars += [cols(attn_norm[l]), cols(ffn_norm[l]), cols(ret_norm[l]), cols(b_gate[l]),
                 taps.reshape(4, FT, P).transpose(2, 1, 0).reshape(P, 4 * FT)]
    pars.append(cols(final_norm))

    consts = np.zeros((P, 6, P), f32)
    row, col = np.arange(P)[:, None], np.arange(P)[None, :]
    consts[:, 0] = row == col
    consts[:, 1] = 1.0
    consts[:, 2] = -0.5
    consts[:, 2, TT:2 * TT] = EPS
    consts[:, 3] = np.where(row >= col, -1.0, 0.0)
    consts[:, 4] = np.where(row >= col, NEG, 0.0)
    inv = f32(10000.0) ** (-np.arange(64, dtype=f32) / f32(64))
    ang = (np.arange(S, dtype=f32)[None, :] * inv[:, None].astype(f32)).astype(f32).astype(np.float64)
    rope = np.stack([np.concatenate([np.cos(ang)] * 2), np.concatenate([np.sin(ang), -np.sin(ang)])], axis=1).astype(f32)
    gamma_log = np.log1p(-np.exp2(-5.0 - np.arange(RET_HEADS)))
    lag = np.arange(S)[None, :] - np.arange(P)[:, None]
    decay = np.where(lag[:, None] >= 0, np.exp(np.maximum(lag, 0)[:, None] * gamma_log[None, :, None]), 0.0) * 128.0 ** -0.5

    arrays = {
        "xt": np.ascontiguousarray(np.asarray(x)[0].T.reshape(KT, P, S).transpose(1, 0, 2)),
        "wts": np.ascontiguousarray(np.concatenate(slabs)),
        "par": np.ascontiguousarray(np.concatenate(pars, axis=1)),
        "consts": consts,
        "rope": rope,
        "decay": decay.astype(f32),
    }
    nc = bacc.Bacc("TRN2", target_bir_lowering=False, num_devices=1)
    aps = [nc.dram_tensor(n, a.shape, mybir.dt.from_np(a.dtype), kind="ExternalInput").ap() for n, a in arrays.items()]
    out = nc.dram_tensor("out", (KT, P, S), F32, kind="ExternalOutput").ap()
    trunk(nc, *aps, out)
    r = run(nc, [arrays], core_ids=[0])
    y = r.results[0]["out"]
    return np.ascontiguousarray(y.reshape(D, S).T).reshape(1, S, D)
```
